# Optimizing a Trainium2 kernel written in Bass

```python
import math
import jax, jax.numpy as jnp
from jax import lax
import numpy as np

D_MODEL = 1024
BATCH = 1
SEQ = 512
DEPTH = 2

CTX_LEN = 256
GRID_W = 64
HEAD_DIM = 64
N_HEADS_A = (D_MODEL // 2) // HEAD_DIM
N_KV_A = N_HEADS_A // 4
GQA_GROUP = N_HEADS_A // N_KV_A
WINDOW = 128
BLOCK = 128
BAND = BLOCK + 2 * WINDOW
CONV_CH = D_MODEL // 4
CONV_W = 3
DIFF_DIM = 32
N_HEADS_C = (D_MODEL // 4) // (2 * DIFF_DIM)
N_EXPERTS = 16
EXPERT_FF = D_MODEL
CAPACITY_FACTOR = 2
ROPE_THETA = 10000.0
EPS = 1e-6
NEG_INF = -1e30

A_Q = N_HEADS_A * HEAD_DIM
A_KV = N_KV_A * HEAD_DIM
C_QK = N_HEADS_C * 2 * DIFF_DIM
C_V = N_HEADS_C * 2 * DIFF_DIM
PROJ_SPLITS = (A_Q, A_KV, A_KV, CONV_CH, CONV_CH, CONV_CH, C_QK, C_QK, C_V)
PROJ_DIM = A_Q + 2 * A_KV + 3 * CONV_CH + 2 * C_QK + C_V
MIX_DIM = A_Q + CONV_CH + C_V

kernel_name = 'hybrid_parallel_heads_ec_moe_dit'

def _rmsnorm(x, g):
    xf = x.astype(jnp.float32)
    y = xf * lax.rsqrt(jnp.mean(xf * xf, axis=-1, keepdims=True) + EPS)
    return (y * g.astype(jnp.float32)).astype(x.dtype)

def _split_proj(p):
    outs, start = [], 0
    for w in PROJ_SPLITS:
        outs.append(p[..., start:start + w])
        start += w
    return outs

def _axial_angles(L, n):
    rows = L // GRID_W
    row = jnp.broadcast_to(jnp.arange(rows, dtype=jnp.float32)[:, None], (rows, GRID_W)).reshape(-1)
    col = jnp.broadcast_to(jnp.arange(GRID_W, dtype=jnp.float32)[None, :], (rows, GRID_W)).reshape(-1)
    inv = ROPE_THETA ** (-jnp.arange(0, n, 2, dtype=jnp.float32) / n)
    return row[:, None] * inv[None, :], col[:, None] * inv[None, :]

def _rotate(x, ang):
    shape = (1, ang.shape[0]) + (1,) * (x.ndim - 3) + (ang.shape[1],)
    cos = jnp.cos(ang).reshape(shape).astype(x.dtype)
    sin = jnp.sin(ang).reshape(shape).astype(x.dtype)
    x1, x2 = jnp.split(x, 2, axis=-1)
    return jnp.concatenate([x1 * cos - x2 * sin, x2 * cos + x1 * sin], axis=-1)

def _rope_2d(x):
    L, d = x.shape[1], x.shape[-1]
    ang_r, ang_c = _axial_angles(L, d // 2)
    xr, xc = jnp.split(x, 2, axis=-1)
    return jnp.concatenate([_rotate(xr, ang_r), _rotate(xc, ang_c)], axis=-1)

def _window_gqa(q, k, v, kc, vc, sink):
    B, L, H, dh = q.shape
    Lc = kc.shape[1]
    nblk = L // BLOCK
    qb = jnp.moveaxis((q * dh ** -0.5).reshape(B, nblk, BLOCK, N_KV_A, GQA_GROUP, dh), 1, 0)
    pad = ((0, 0), (WINDOW, WINDOW), (0, 0), (0, 0))
    kp = jnp.pad(k, pad)
    vp = jnp.pad(v, pad)
    sink_l = jnp.broadcast_to(sink.astype(jnp.float32).reshape(1, N_KV_A, GQA_GROUP, 1, 1),
                              (B, N_KV_A, GQA_GROUP, BLOCK, 1))

    def block(args):
        qi, i = args
        start = i * BLOCK
        kb = lax.dynamic_slice_in_dim(kp, start, BAND, axis=1)
        vb = lax.dynamic_slice_in_dim(vp, start, BAND, axis=1)
        qpos = start + jnp.arange(BLOCK)
        kpos = start - WINDOW + jnp.arange(BAND)
        ok = (jnp.abs(qpos[:, None] - kpos[None, :]) <= WINDOW) & (kpos >= 0)[None, :] & (kpos < L)[None, :]
        s_loc = jnp.einsum('bqkgd,bskd->bkgqs', qi, kb).astype(jnp.float32)
        s_loc = jnp.where(ok, s_loc, NEG_INF)
        s_ctx = jnp.einsum('bqkgd,bckd->bkgqc', qi, kc).astype(jnp.float32)
        p = jax.nn.softmax(jnp.concatenate([s_ctx, s_loc, sink_l], axis=-1), axis=-1).astype(v.dtype)
        return (jnp.einsum('bkgqc,bckd->bqkgd', p[..., :Lc], vc)
                + jnp.einsum('bkgqs,bskd->bqkgd', p[..., Lc:Lc + BAND], vb))

    out = lax.map(block, (qb, jnp.arange(nblk)))
    return jnp.moveaxis(out, 0, 1).reshape(B, L, H * dh)

def _ctx_gqa(qc, kc, vc, sink):
    B, Lc, H, dh = qc.shape
    qg = (qc * dh ** -0.5).reshape(B, Lc, N_KV_A, GQA_GROUP, dh)
    s = jnp.einsum('bqkgd,bckd->bkgqc', qg, kc).astype(jnp.float32)
    sink_l = jnp.broadcast_to(sink.astype(jnp.float32).reshape(1, N_KV_A, GQA_GROUP, 1, 1),
                              (B, N_KV_A, GQA_GROUP, Lc, 1))
    p = jax.nn.softmax(jnp.concatenate([s, sink_l], axis=-1), axis=-1)[..., :Lc].astype(vc.dtype)
    return jnp.einsum('bkgqc,bckd->bqkgd', p, vc).reshape(B, Lc, H * dh)

def _short_conv(h, gb, gc, w):
    L = h.shape[1]
    half = CONV_W // 2
    up = jnp.pad(gc * h, ((0, 0), (half, half), (0, 0)))
    y = sum(up[:, j:j + L] * w[j] for j in range(CONV_W))
    return gb * y

def _diff_weights(qi, K, lam):
    d = qi.shape[-1]
    s = jnp.einsum('bqhjd,bkhjd->bhjqk', qi * d ** -0.5, K).astype(jnp.float32)
    p = jax.nn.softmax(s, axis=-1)
    return p[:, :, 0] - lam * p[:, :, 1]

def _diff_attn_latent(q, k, v, kc, vc, lam):
    B, L, H, _, d = q.shape
    K = jnp.concatenate([kc, k], axis=1)
    V = jnp.concatenate([vc, v], axis=1)
    qb = jnp.moveaxis(q.reshape(B, L // BLOCK, BLOCK, H, 2, d), 1, 0)

    def block(qi):
        a = _diff_weights(qi, K, lam).astype(V.dtype)
        return jnp.einsum('bhqk,bkhe->bqhe', a, V)

    out = lax.map(block, qb)
    return jnp.moveaxis(out, 0, 1).reshape(B, L, H, 2 * d)

def _diff_attn_ctx(qc, kc, vc, lam):
    a = _diff_weights(qc, kc, lam).astype(vc.dtype)
    return jnp.einsum('bhqk,bkhe->bqhe', a, vc)

def _mixer(hx, hc, w_in, w_out, sink, conv_w, lam_p, subln, lam_init, need_ctx):
    B, L, _ = hx.shape
    Lc = hc.shape[1]
    qa, ka, va, cin, cb, cc, qd, kd, vd = _split_proj(hx @ w_in)
    qa_c, ka_c, va_c, cin_c, cb_c, cc_c, qd_c, kd_c, vd_c = _split_proj(hc @ w_in)
    ka_c = ka_c.reshape(B, Lc, N_KV_A, HEAD_DIM)
    va_c = va_c.reshape(B, Lc, N_KV_A, HEAD_DIM)
    ya = _window_gqa(_rope_2d(qa.reshape(B, L, N_HEADS_A, HEAD_DIM)),
                     _rope_2d(ka.reshape(B, L, N_KV_A, HEAD_DIM)),
                     va.reshape(B, L, N_KV_A, HEAD_DIM), ka_c, va_c, sink)
    yb = _short_conv(cin, cb, cc, conv_w)
    lp = lam_p.astype(jnp.float32)
    lam = jnp.exp(jnp.sum(lp[0] * lp[1])) - jnp.exp(jnp.sum(lp[2] * lp[3])) + lam_init
    kd_c = kd_c.reshape(B, Lc, N_HEADS_C, 2, DIFF_DIM)
    vd_c = vd_c.reshape(B, Lc, N_HEADS_C, 2 * DIFF_DIM)
    yd = _diff_attn_latent(_rope_2d(qd.reshape(B, L, N_HEADS_C, 2, DIFF_DIM)),
                           _rope_2d(kd.reshape(B, L, N_HEADS_C, 2, DIFF_DIM)),
                           vd.reshape(B, L, N_HEADS_C, 2 * DIFF_DIM), kd_c, vd_c, lam)
    yd = (_rmsnorm(yd, subln) * (1.0 - lam_init)).reshape(B, L, C_V)
    out_x = jnp.concatenate([ya, yb, yd], axis=-1) @ w_out
    if not need_ctx:
        return out_x, None
    yac = _ctx_gqa(qa_c.reshape(B, Lc, N_HEADS_A, HEAD_DIM), ka_c, va_c, sink)
    ybc = _short_conv(cin_c, cb_c, cc_c, conv_w)
    ydc = _diff_attn_ctx(qd_c.reshape(B, Lc, N_HEADS_C, 2, DIFF_DIM), kd_c, vd_c, lam)
    ydc = (_rmsnorm(ydc, subln) * (1.0 - lam_init)).reshape(B, Lc, C_V)
    out_c = jnp.concatenate([yac, ybc, ydc], axis=-1) @ w_out
    return out_x, out_c

def _ec_moe(h, router, w_gate, w_up, w_down):
    B, n, _ = h.shape
    cap = CAPACITY_FACTOR * n // N_EXPERTS
    aff = jax.nn.softmax((h @ router).astype(jnp.float32), axis=-1)
    g, idx = lax.top_k(jnp.swapaxes(aff, 1, 2), cap)
    bidx = jnp.arange(B)[:, None, None]
    xs = h[bidx, idx]
    a = jnp.einsum('becd,edf->becf', xs, w_gate)
    u = jnp.einsum('becd,edf->becf', xs, w_up)
    y = jnp.einsum('becf,efd->becd', jax.nn.silu(a) * u, w_down) * g[..., None].astype(h.dtype)
    return jnp.zeros_like(h).at[bidx, idx].add(y)

def setup_inputs(seed: int = 0) -> dict:
    key = jax.random.key(seed)
    ks = jax.random.split(key, 20)
    D = D_MODEL
    f32 = jnp.float32

    def nrm(k, shape, s):
        return jax.random.normal(k, shape, f32) * s

    return {
        'x': nrm(ks[0], (BATCH, SEQ, D), 1.0),
        'c': nrm(ks[1], (BATCH, D), 1.0),
        'ctx': nrm(ks[2], (BATCH, CTX_LEN, D), 1.0),
        'c_ctx': nrm(ks[3], (D,), 1.0),
        'w_ada': nrm(ks[4], (DEPTH, D, 6 * D), 0.5 * D ** -0.5),
        'b_ada': nrm(ks[5], (DEPTH, 6 * D), 0.02),
        'norm1': 1.0 + nrm(ks[6], (DEPTH, D), 0.02),
        'norm2': 1.0 + nrm(ks[7], (DEPTH, D), 0.02),
        'w_in': nrm(ks[8], (DEPTH, D, PROJ_DIM), D ** -0.5),
        'w_out': nrm(ks[9], (DEPTH, MIX_DIM, D), MIX_DIM ** -0.5),
        'attn_sink': nrm(ks[10], (DEPTH, N_HEADS_A), 0.5),
        'conv_w': nrm(ks[11], (DEPTH, CONV_W, CONV_CH), CONV_W ** -0.5),
        'diff_lambda': nrm(ks[12], (DEPTH, 4, DIFF_DIM), 0.1),
        'diff_subln': 1.0 + nrm(ks[13], (DEPTH, 2 * DIFF_DIM), 0.02),
        'router': nrm(ks[14], (DEPTH, D, N_EXPERTS), D ** -0.5),
        'w_gate': nrm(ks[15], (DEPTH, N_EXPERTS, D, EXPERT_FF), D ** -0.5),
        'w_up': nrm(ks[16], (DEPTH, N_EXPERTS, D, EXPERT_FF), D ** -0.5),
        'w_down': nrm(ks[17], (DEPTH, N_EXPERTS, EXPERT_FF, D), EXPERT_FF ** -0.5),
        'norm_final': 1.0 + nrm(ks[18], (D,), 0.02),
    }

def reference(x, c, ctx, c_ctx, w_ada, b_ada, norm1, norm2, w_in, w_out, attn_sink, conv_w,
              diff_lambda, diff_subln, router, w_gate, w_up, w_down, norm_final):
    silu_c = jax.nn.silu(c)
    silu_cc = jax.nn.silu(c_ctx)
    for l in range(DEPTH):
        need_ctx = l < DEPTH - 1
        mod_x = silu_c @ w_ada[l] + b_ada[l]
        mod_c = silu_cc @ w_ada[l] + b_ada[l]
        sh1, sc1, g1, sh2, sc2, g2 = jnp.split(mod_x[:, None, :], 6, axis=-1)
        csh1, csc1, cg1, csh2, csc2, cg2 = jnp.split(mod_c, 6, axis=-1)
        lam_init = 0.8 - 0.6 * math.exp(-0.3 * l)
        hx = _rmsnorm(x, norm1[l]) * (1.0 + sc1) + sh1
        hc = _rmsnorm(ctx, norm1[l]) * (1.0 + csc1) + csh1
        ox, oc = _mixer(hx, hc, w_in[l], w_out[l], attn_sink[l], conv_w[l], diff_lambda[l],
                        diff_subln[l], lam_init, need_ctx)
        x = x + g1 * ox
        hx2 = _rmsnorm(x, norm2[l]) * (1.0 + sc2) + sh2
        x = x + g2 * _ec_moe(hx2, router[l], w_gate[l], w_up[l], w_down[l])
        if need_ctx:
            ctx = ctx + cg1 * oc
            hc2 = _rmsnorm(ctx, norm2[l]) * (1.0 + csc2) + csh2
            ctx = ctx + cg2 * _ec_moe(hc2, router[l], w_gate[l], w_up[l], w_down[l])
    return _rmsnorm(x, norm_final)


_drawn_inputs = setup_inputs


def setup_inputs(seed=0):
    import zlib

    import numpy as np

    out = dict(_drawn_inputs(seed))
    spreads = {}
    factors = {'norm1': 5.367,
     'norm2': 6.235,
     'attn_sink': 8.0,
     'diff_subln': 190.915,
     'norm_final': 23.819,
     'diff_lambda': 2.739}
    for name, (base, spread) in spreads.items():
        noise = np.random.default_rng([zlib.crc32(name.encode()), seed]).standard_normal(out[name].shape)
        drawn = base * np.exp(spread * noise) if base else spread * noise
        out[name] = __import__('jax').numpy.asarray(drawn.astype(out[name].dtype))
    for name, factor in factors.items():
        out[name] = (out[name] * factor).astype(out[name].dtype)
    return out
```

```python
import math
from contextlib import ExitStack

import numpy as np

import concourse.bass as bass
from concourse import mybir

F32 = mybir.dt.float32
BF16 = mybir.dt.bfloat16
U32 = mybir.dt.uint32
ALU = mybir.AluOpType
ACT = mybir.ActivationFunctionType
AX_X = mybir.AxisListType.X

P = 128
GRID_W = 64
ROPE_THETA = 10000.0
EPS = 1e-6
MASKED = -1e30
RING = 12
SLOT = 2048
HEAD = 64
DIFF = 32
CAPACITY_FACTOR = 2
CONV_W = 3

def rope_tables(seq):
    pos = np.arange(seq)
    parts = []
    for dim in (HEAD, DIFF):
        half = dim // 2
        inv = (np.float32(ROPE_THETA) ** (-np.arange(0, half, 2, dtype=np.float32) / np.float32(half))).astype(np.float32)
        cos, sin = [], []
        for axis in ((pos // GRID_W).astype(np.float32), (pos % GRID_W).astype(np.float32)):
            ang = (axis[:, None] * inv[None, :]).astype(np.float32)
            c, s = np.cos(ang).astype(np.float32), np.sin(ang).astype(np.float32)
            cos += [c, c]
            sin += [-s, s]
        parts += [np.concatenate(cos, 1), np.concatenate(sin, 1)]
    tab = np.concatenate(parts, 1)
    return np.ascontiguousarray(tab.reshape(seq // P, P, -1).transpose(1, 0, 2))

def build_program(nc, x, c, ctx, c_ctx, w_ada, b_ada, norm1, norm2, w_in, w_out, attn_sink, conv_w,
                  diff_lambda, diff_subln, router, w_gate, w_up, w_down, norm_final, rope, out):
    DEPTH, D, PROJ = w_in.shape
    SEQ, CTX = x.shape[1], ctx.shape[1]
    NX, NC = SEQ // P, CTX // P
    NB = NX + NC
    T = NB * P
    KD = D // P
    NE = router.shape[2]
    F = w_gate.shape[3]
    KF = F // P
    CAPX, CAPC = CAPACITY_FACTOR * SEQ // NE, CAPACITY_FACTOR * CTX // NE
    CAP = CAPX + CAPC
    HW = attn_sink.shape[1]
    NKV = HW // 4
    PAIRS = HW // 2
    HD = conv_w.shape[2] // (2 * DIFF)
    NG = 2 * HD
    assert (D, F, KD, NX, NC, NE, HW, HD, PROJ) == (1024, 1024, 8, 4, 2, 16, 8, 4, 2304)
    assert (CAPX, CAPC) == (64, 32)
    UNITS_E = 12

    es = ExitStack()

    def sb(name, shape, dt=F32):
        return es.enter_context(nc.sbuf_tensor(name, shape, dt))

    def sem(name):
        return es.enter_context(nc.semaphore(name))

    res = nc.dram_tensor("residual", (T, D), F32, kind="Internal").ap()
    xnd = nc.dram_tensor("normed_rows", (T, D), F32, kind="Internal").ap()

    ring = sb("ring", [P, RING, SLOT])
    arena = sb("arena", [P, 25348])
    BIG = 7680

    def area(off, *dims):
        n = int(np.prod(dims))
        ap = arena[:, off:off + n]
        if len(dims) == 2:
            ap = ap.rearrange("p (a b) -> p a b", a=dims[0])
        return ap

    hT = area(0, 8, T)
    PT = [area(4 * T, 6, P), area(5 * T, 6, P)]
    convo = area(6144, 2, T)
    qT = area(BIG, 4, T)
    kTp = area(BIG + 3072, 2, T)
    v_sb = area(BIG + 4608, NB, P)
    qdT = area(BIG + 5376, 2, T)
    vd_sb = area(BIG + 6912, NB, 256)
    kdp = area(BIG + 8448, NG, T)
    WK = BIG + 14592
    prob = [area(WK + 769 * n, 769) for n in range(4)]
    ropet = area(WK, NX, 192)
    rtmp = area(WK + 768, 512)
    rq = [area(WK + 1280 + 512 * n, 512) for n in range(2)]
    kraw = area(WK + 2304, P)
    rk = [area(WK + 2432 + P * n, P) for n in range(2)]
    PADX, PADC = SEQ + 2, CTX + 2
    upad = area(WK, 2, PADX + PADC)
    ytmp = area(WK + 1544, PADX + PADC - 2)
    n_x = [area(BIG + 8448 + D * n, D) for n in range(3)]
    n_n = [area(BIG + 8448 + 3072 + D * n, D) for n in range(2)]
    n_j = area(BIG + 8448 + 5120, D)
    o_x = [area(BIG + D * n, D) for n in range(3)]
    o_n = [area(BIG + 3072 + D * n, D) for n in range(2)]
    o_h = [area(BIG + 5120 + D * n, 8, P) for n in range(2)]
    g1row = [area(BIG + 7168, D), area(BIG + 8192, D)]
    o_t = area(BIG + 9216, D)
    xg = area(BIG + 10240, D)
    xsT = area(BIG + 11264, 8, CAP)
    sg = area(BIG + 12032, 8, CAP)
    hE = area(BIG + 12800, 8, CAP)
    yg = area(BIG + 13568, D)
    g2row = area(BIG + 14592, D)
    work = area(BIG + 15616, SEQ)
    srt = area(WK + 1024, 2, T)
    sqd = area(4 * T, 2, T)

    ident = sb("ident", [P, P])
    identb = sb("identb", [P, P], BF16)
    masks = sb("masks", [P, 2, P], BF16)
    halves = sb("halves", [P, P])
    sel = sb("sel", [48, NE])
    eps = sb("eps", [P, 1])
    diag = sb("diag", [P, 4, P])
    packr = arena[0:62, 0:P]
    packb = arena[0:96, P:2 * P]
    pack = sb("pack", [P, 62])
    bcol = sb("bcol", [P, DEPTH, 48])
    cs = sb("cs", [P, KD, 2])
    modrow = sb("modrow", [2, 512])
    mod = sb("mod", [P, DEPTH, 48, 2])
    acol = sb("acol", [P, DEPTH, 2, KD, 2])
    sinkb = sb("sinkb", [P, DEPTH, HW])
    lamr = arena[:, 2 * P:2 * P + DEPTH * 4 * DIFF]
    lamp = sb("lamp", [P, DEPTH, 2, DIFF])
    lam2 = sb("lam2", [P, DEPTH, 2])
    nlam = sb("nlam", [P, DEPTH])
    sublc = sb("sublc", [P, DEPTH])
    stat = sb("stat", [P, 3, NB])
    smx = sb("smx", [P, 3, 8])
    rout = sb("rout", [P, DEPTH, KD, NE])
    aff = sb("aff", [P, NB, NE])
    affm = sb("affm", [P, 2, NB])
    aff48 = sb("aff48", [P, NX, 48])
    vals = sb("vals", [48, CAPX])
    idx = sb("idx", [48, CAPX], U32)
    vpad = sb("vpad", [48, CAP])
    ipad = sb("ipad", [48, CAP])
    gT = sb("gT", [CAP, NE + 1])
    iT = sb("iT", [CAP, NE + 1], U32)
    gcur = sb("gcur", [CAP, 1])
    gidx = sb("gidx", [CAP, 1], U32)
    sidx = sb("sidx", [CAP, 1], U32)
    perch = sb("perch", [1, 4, 2])

    psum = es.enter_context(nc.psum_tensor("psum", [P, 4096], F32))

    def bank(b, n=512, off=0):
        return psum[:, b * 512 + off:b * 512 + off + n]

    units = []
    where = {}

    def plan(key, srcs):
        where[key] = len(units)
        units.extend(srcs)

    def ada_units(l, g):
        v = w_ada[l].rearrange("(h k p) n -> h p k n", p=P, k=4)
        return [(v[h, :, :, g * 512:(g + 1) * 512], 4) for h in range(2)]

    def win_units(l):
        v = w_in[l].rearrange("(k p) n -> p k n", p=P)
        order = [0, 1, 2, 6, 7, 8, 3, 5, 4]
        return [(v[:, :, 256 * j:256 * j + 256], 8) for j in order]

    def wout_units(l):
        v = w_out[l].rearrange("(h k p) n -> h p k n", p=P, k=2)
        return [(v[h], 2) for h in range(4)]

    ADA_REST = [(0, g) for g in range(4, 12)] + [(l, g) for l in range(1, DEPTH) for g in range(12)]
    for g in range(4):
        plan(("ada", 0, g), ada_units(0, g))
    for l in range(DEPTH):
        plan(("win", l), win_units(l))
        if l == 0:
            for lg in ADA_REST:
                plan(("ada",) + lg, ada_units(*lg))
        plan(("wout", l), wout_units(l))
        plan(("exp", l), [None] * (UNITS_E * NE))

    free = sem("ring_free")
    landed = [sem(f"ring_landed{s}") for s in range(RING)]

    def slot(n, k):
        return ring[:, n % RING, :].rearrange("p (k m) -> p k m", k=k)

    def arrive(e, n):
        e.wait_ge(landed[n % RING], 16 * (n // RING + 1))

    s_const = sem("const_made")
    s_cload = sem("const_loaded")
    s_rout = sem("router_loaded")
    s_pack = sem("pack_transposed")
    s_packc = sem("pack_copied")
    s_cs = sem("silu_ready")
    s_row = sem("ada_row")
    s_adaT = sem("ada_transposed")
    s_col = sem("ada_col")
    s_lamx = sem("lambda_sums")
    dch = sem("dve_chain")
    ach = sem("act_chain")
    pch = sem("pool_chain")
    s_acol = sem("norm_scales")
    s_lam = sem("lambda_ready")
    s_nf = sem("final_gain_loaded")
    f_in = [sem(f"final_in{j}") for j in range(3)]
    f_rms = sem("final_rms")
    f_out = sem("final_scaled")
    s_end = sem("out_stored")
    chains = {"d": 0, "a": 0, "p": 0}

    def dlink(e, ins):
        chains["d"] += 1
        ins.then_inc(dch, 1)
        e.wait_ge(dch, chains["d"])

    def alink(e, ins):
        chains["a"] += 1
        ins.then_inc(ach, 1)
        e.wait_ge(ach, chains["a"])

    def plink(e, ins):
        chains["p"] += 1
        ins.then_inc(pch, 1)
        e.wait_ge(pch, chains["p"])

    def nq(l):
        return NB if l < DEPTH - 1 else NX
    class Unit:
        pass

    def attention(l):
        items, us = [], []
        for kind in "DW":
            for b in range(nq(l)):
                for h in range(HD if kind == "D" else HW):
                    it = Unit()
                    it.kind, it.b, it.h, it.m = kind, b, h, len(items)
                    if b >= NX:
                        it.blocks = list(range(NX, NB))
                    elif kind == "D":
                        it.blocks = list(range(NB))
                    else:
                        it.blocks = list(range(NX, NB)) + [j for j in (b - 1, b, b + 1) if 0 <= j < NX]
                    it.first = len(us)
                    for j in range(2 if kind == "D" else 1):
                        u = Unit()
                        u.item, u.j, u.u = it, j, len(us)
                        u.width = P * len(it.blocks) + (kind == "W")
                        us.append(u)
                    it.last = len(us) - 1
                    it.over = (items[-1].over if items else 0) + (len(it.blocks) > 4)
                    items.append(it)
        return items, us

    ATT = [attention(l) for l in range(DEPTH)]
    def signals(l):
        nu, ni, n = len(ATT[l][1]), len(ATT[l][0]), nq(l)
        s = dict.fromkeys("xn rt nt hd ha kvc ta ke vdc tb kde".split(), NB)
        s |= dict.fromkeys("pa pb".split(), NB - 1)
        s |= dict.fromkeys("rope ropeb".split(), NX)
        s |= dict.fromkeys("qe qde x1 ort orc oxn ot od oa lg".split(), n)
        s |= dict.fromkeys("S nm exp diag".split(), nu)
        s |= dict.fromkeys("T c4 AV".split(), ni)
        s |= dict.fromkeys("kz cu cuc cy".split(), 2)
        s |= dict.fromkeys("dsq dss drt dsub asub aexp aff aT pad rows ri".split(), 1)
        s |= dict.fromkeys("xt xm xs gc silu he yg".split(), NE)
        gates = 3 if l < DEPTH - 1 else 2
        s |= dict(tab=16, pc=3, c5=ATT[l][0][-1].over, mix=ni // 2, gx=gates, gxe=gates, po=n - 1,
                  gat=16 * (NE + 1), sc=16 * NE, yf=NE + 1, gi=2 * NE)
        s |= {f"nx{j}": 16 * len(range(j, NB, 3)) for j in range(3)}
        s |= {f"{name}{j}": 16 * len(range(j, n, 3)) for j in range(3) for name in ("ox", "stx")}
        s |= {f"stn{j}": 16 * len(range(j, n, 2)) for j in range(2)}
        return s

    SIGNALS = [signals(l) for l in range(DEPTH)]
    stage_sem = {name: sem(name) for name in SIGNALS[0]}

    class Layer:

        def __init__(self, l):
            self.base = {name: sum(SIGNALS[j][name] for j in range(l)) for name in stage_sem}

        def __getitem__(self, name):
            return stage_sem[name]

        def __call__(self, name, value):
            return stage_sem[name], value + self.base[name]

    LS = [Layer(l) for l in range(DEPTH)]


    NU0 = len(ATT[0][1])
    every = (NU0 - 4) // len(ADA_REST)
    assert every >= 3
    ADA_AT = {1 + every * n: n for n in range(len(ADA_REST))}

    def mixc(k):
        return convo[:, k - 4, :] if k in (4, 5) else hT[:, k, :]

    def item_of(l, u):
        return ATT[l][1][u].item

    def toks(b):
        return slice(b * P, (b + 1) * P)

    def stream(b):
        return 0 if b < NX else 1

    def lam_init(l):
        return 0.8 - 0.6 * math.exp(-0.3 * l)

    def done_a(l, t):
        return LS[l]("pa", t + 1) if t < NB - 1 else (free, where[("win", l)] + 3)

    def done_b(l, t):
        return LS[l]("pb", t + 1) if t < NB - 1 else (free, where[("win", l)] + 6)

    def done_c(l, j):
        return LS[l]("pc", j // 2 + 1) if j % 2 == 0 else (free, where[("win", l)] + 7 + j // 2)

    def done_o(l, t):
        return LS[l]("po", t + 1) if t < nq(l) - 1 else (free, where[("wout", l)] + 4)

    ada_order = [(0, g) for g in range(4)] + ADA_REST

    block = es.enter_context(nc.Block())

    @block.sync
    def _(sp):
        def load(n):
            if n >= RING:
                sp.wait_ge(free, n - RING + 1)
            src, k = units[n]
            sp.dma_start(slot(n, k), src).then_inc(landed[n % RING], 16)

        n = 0
        for l in range(DEPTH):
            base = where[("exp", l)]
            while n < base:
                load(n)
                n += 1
            wv = [w[l].rearrange("e (h k p) f -> e h p k f", p=P, k=2) for w in (w_gate, w_up, w_down)]
            with sp.Fori(0, NE) as e:
                for q in range(UNITS_E):
                    sp.wait_ge(free, e * UNITS_E + (base + q - RING + 1))
                    sp.dma_start(slot(base + q, 2), wv[q // 4][bass.ds(e, 1), q % 4]
                                 ).then_inc(landed[(base + q) % RING], 16)
            n = base + UNITS_E * NE

    @block.gpsimd
    def _(pool):
        pool.memset(ident[:], 0.0)
        pool.memset(identb[:], 0.0)
        pool.memset(masks[:], 0.0)
        pool.memset(sel[:], 0.0)
        pool.memset(eps[:], EPS)
        pool.memset(vpad[:], 0.0)
        pool.memset(perch[:], 0.0)
        pool.memset(aff48[:], -1.0)
        plink(pool, pool.memset(ipad[:], 0.0))
        for t in (ident, identb):
            pool.affine_select(out=t[:], in_=t[:], compare_op=ALU.not_equal, fill=1.0, base=0,
                               pattern=[[-1, P]], channel_multiplier=1)
        pool.affine_select(out=masks[:, 0, :], in_=masks[:, 0, :], compare_op=ALU.is_ge, fill=MASKED, base=0,
                           pattern=[[1, P]], channel_multiplier=-1)
        pool.affine_select(out=masks[:, 1, :], in_=masks[:, 1, :], compare_op=ALU.is_ge, fill=MASKED, base=0,
                           pattern=[[-1, P]], channel_multiplier=1)
        plink(pool, pool.affine_select(out=sel[:], in_=sel[:], compare_op=ALU.not_equal, fill=1.0, base=0,
                                       pattern=[[-1, NE]], channel_multiplier=1))
        pool.affine_select(out=sel[:], in_=sel[:], compare_op=ALU.not_equal, fill=1.0, base=-32,
                           pattern=[[-1, NE]], channel_multiplier=1).then_inc(s_const, 1)

        for l in range(DEPTH):
            L = LS[l]

            def rows(b):
                if l == 0:
                    return x[0, toks(b), :] if b < NX else ctx[0, (b - NX) * P:(b - NX + 1) * P, :]
                return res[toks(b), :]

            if l:
                pool.wait_ge(*LS[l - 1]("sc", 16 * NE))
            pool.dma_start(ropet, rope).then_inc(L["tab"], 16)
            for t in range(NB):
                if t >= 3:
                    pool.wait_ge(*L("xn", t - 2))
                pool.dma_start(n_x[t % 3], rows(t)).then_inc(L[f"nx{t % 3}"], 16)
                if t == 2:
                    pool.memset(kTp, 0.0).then_inc(L["kz"], 1)
            pool.wait_ge(*L("nt", NB))
            pool.memset(kdp, 0.0).then_inc(L["kz"], 1)

            pool.wait_ge(*L("AV", len(ATT[l][0])))
            for t in range(3):
                pool.dma_start(o_x[t % 3], rows(t)).then_inc(L[f"ox{t % 3}"], 16)
            for t in range(nq(l)):
                pool.wait_ge(*L("x1", t + 1))
                pool.dma_start(res[toks(t), :], o_x[t % 3]).then_inc(L[f"stx{t % 3}"], 16)
                pool.wait_ge(*L("oxn", t + 1))
                pool.dma_start(xnd[toks(t), :], o_n[t % 2]).then_inc(L[f"stn{t % 2}"], 16)
                if t + 3 < nq(l):
                    pool.wait_ge(*L(f"stx{t % 3}", 16 * (t // 3 + 1)))
                    pool.dma_start(o_x[t % 3], rows(t + 3)).then_inc(L[f"ox{t % 3}"], 16)
            for j in range(3):
                pool.wait_ge(*L(f"stx{j}", 16 * len(range(j, nq(l), 3))))
            for j in range(2):
                pool.wait_ge(*L(f"stn{j}", 16 * len(range(j, nq(l), 2))))

            n_tok = CAP if l < DEPTH - 1 else CAPX
            pool.wait_ge(*L("ri", 1))
            plink(pool, pool.tensor_copy(gidx[0:n_tok, :], iT[0:n_tok, 0:1]))

            def gather():
                pool.indirect_dma_start(out=xg[0:n_tok, :], out_offset=None, in_=xnd,
                                        in_offset=bass.IndirectOffsetOnAxis(ap=gidx[0:n_tok, 0:1], axis=0)
                                        ).then_inc(L["gat"], 16)

            gather()
            pool.sem_inc(L["yf"], 1)

            def idle(n):
                return pool.tensor_tensor(perch[:, n, :], perch[:, 3, :], perch[:, 3, :], ALU.add)

            with pool.Fori(0, NE) as e:
                pool.wait_ge(*L("gat", e * 16 + 16))
                pool.wait_ge(*L("xt", e + 1))
                pool.tensor_copy(gidx[0:n_tok, :], iT[0:n_tok, bass.ds(e + 1, 1)]).then_inc(L["gi"], 1)
                pool.wait_ge(*L("gi", e * 2 + 1))
                idle(0)
                gather()
                pool.wait_ge(*L("yg", e + 1))
                pool.tensor_copy(sidx[0:n_tok, :], iT[0:n_tok, bass.ds(e, 1)]).then_inc(L["gi"], 1)
                pool.wait_ge(*L("gi", e * 2 + 2))
                idle(1)
                pool.indirect_dma_start(out=res, out_offset=bass.IndirectOffsetOnAxis(ap=sidx[0:n_tok, 0:1], axis=0),
                                        in_=yg[0:n_tok, :], in_offset=None, compute_op=ALU.add
                                        ).then_inc(L["sc"], 16)
                pool.wait_ge(*L("sc", e * 16 + 16))
                idle(2).then_inc(L["yf"], 1)
            pool.wait_ge(*L("gat", 16 * (NE + 1)))

        pool.wait_ge(*LS[DEPTH - 1]("sc", 16 * NE))
        pool.dma_start(g1row[0], norm_final.rearrange("(a n) -> a n", a=1).broadcast_to([P, D])).then_inc(s_nf, 16)
        for t in range(3):
            pool.dma_start(o_x[t], res[toks(t), :]).then_inc(f_in[t % 3], 16)
        for t in range(NX):
            pool.wait_ge(f_out, t + 1)
            pool.dma_start(out[0, toks(t), :], o_x[t % 3]).then_inc(s_end, 16)
            if t + 3 < NX:
                pool.wait_ge(s_end, 16 * (t + 1))
                pool.dma_start(o_x[t % 3], res[toks(t + 3), :]).then_inc(f_in[t % 3], 16)
        pool.wait_ge(s_end, 16 * NX)

    @block.scalar
    def _(act):
        loads = [(packr[0:8, :], c[0].rearrange("(k p) -> k p", p=P)),
                 (packr[8:16, :], c_ctx.rearrange("(k p) -> k p", p=P)),
                 (packr[16:32, :], norm1.rearrange("l (k p) -> (l k) p", p=P)),
                 (packr[32:48, :], norm2.rearrange("l (k p) -> (l k) p", p=P)),
                 (packr[48:60, :], conv_w.rearrange("l j (k p) -> (l j k) p", p=P)),
                 (packr[60:62, 0:64], diff_subln), (packr[60:62, 64:128], diff_subln),
                 (packb, b_ada.rearrange("l (k p) -> (l k) p", p=P)),
                 (sinkb[:].rearrange("p l h -> p (l h)"),
                  attn_sink.rearrange("(a l) h -> a (l h)", a=1).broadcast_to([P, DEPTH * HW])),
                 (lamr, diff_lambda.rearrange("(a l) j d -> a (l j d)", a=1).broadcast_to([P, DEPTH * 4 * DIFF]))]
        for o, i in loads:
            act.dma_start(o, i).then_inc(s_cload, 16)
        for l in range(DEPTH):
            act.dma_start(rout[:, l], router[l].rearrange("(k p) e -> p k e", p=P)).then_inc(s_rout, 16)
        act.wait_ge(s_packc, 1)
        act.activation(cs[:].rearrange("p k s -> p s k"), pack[:, 0:16].rearrange("p (s k) -> p s k", s=2),
                       ACT.Silu).then_inc(s_cs, 1)
        act.wait_ge(s_lamx, 1)
        act.activation(lam2[:], lam2[:], ACT.Exp).then_inc(s_lam, 1)
        act.wait_ge(s_const, 1)

        for l in range(DEPTH):
            L = LS[l]
            for i in range(NB + 2):
                if i < NB:
                    t, s = i, stream(i)
                    act.wait_ge(*L(f"nx{t % 3}", 16 * (t // 3 + 1)))
                    alink(act, act.activation(n_j, n_x[t % 3], ACT.Square, accum_out=stat[:, 0, t:t + 1]))
                    act.activation(stat[:, 1, t:t + 1], stat[:, 0, t:t + 1], ACT.Sqrt, bias=eps[:], scale=1.0 / D
                                   ).then_inc(L["rt"], 1)
                    act.wait_ge(s_acol, 2 * l + 1)
                    act.wait_ge(*L("nt", t + 1))
                    for k in range(4, 8):
                        ins = act.activation(hT[:, k, toks(t)], bank(1, P, (k - 4) * P), ACT.Identity,
                                             bias=mod[:, l, k, s:s + 1], scale=acol[:, l, 0, k, s:s + 1])
                    ins.then_inc(L["ha"], 1)
                if 1 <= i <= NB:
                    t = i - 1
                    act.wait_ge(*done_a(l, t))
                    kb = 4 + t % 2
                    if t >= 2:
                        act.wait_ge(*L("ta", t - 1))
                    if t < NX:
                        if t >= 1:
                            act.wait_ge(*L("rope", t))
                        act.activation(kraw, bank(kb, P), ACT.Copy)
                    else:
                        act.activation(rk[t % 2], bank(kb, P), ACT.Copy)
                        if l < DEPTH - 1:
                            act.activation(rq[t % 2].rearrange("p (a s d) -> p s a d", s=2, d=HEAD),
                                           bank(2 + t % 2).rearrange("p (s a d) -> p s a d", s=2, d=HEAD), ACT.Copy)
                    act.activation(v_sb[:, t, :], bank(kb, P, P), ACT.Copy).then_inc(L["kvc"], 1)
                if i >= 2:
                    t = i - 2
                    if t < nq(l):
                        act.wait_ge(*L("ta", t + 1))
                        act.activation(qT[:, :, toks(t)], bank(6).rearrange("p (a m) -> p a m", a=4), ACT.Copy,
                                       scale=HEAD ** -0.5).then_inc(L["qe"], 1)
            for i in range(NB + 1):
                if i < NB:
                    t = i
                    act.wait_ge(*done_b(l, t))
                    act.activation(vd_sb[:, t, :], bank(4 + t % 2, 256), ACT.Copy)
                    if t >= NX:
                        act.wait_ge(*L("tb", t - 1))
                        q0 = 0 if l < DEPTH - 1 else 256
                        act.activation(rq[t % 2][:, q0:512], bank(2 + t % 2, 512 - q0, q0), ACT.Copy)
                    act_last = act.activation(stat[:, 0, t:t + 1], eps[:], ACT.Copy)
                    act_last.then_inc(L["vdc"], 1)
                if i >= 1 and i - 1 < nq(l):
                    t = i - 1
                    act.wait_ge(*L("tb", t + 1))
                    act.activation(qdT[:, :, toks(t)], bank(6, 256).rearrange("p (a m) -> p a m", a=2), ACT.Copy,
                                   scale=DIFF ** -0.5).then_inc(L["qde"], 1)
            act.wait_ge(*L("ropeb", NX))
            act.wait_ge(*L("tb", NB))
            for cc in range(2):
                act.wait_ge(*done_c(l, cc))
                if l < DEPTH - 1:
                    act.activation(upad[:, cc, PADX + 1:PADX + 1 + CTX], bank(4 + cc, CTX), ACT.Copy)
                act.activation(upad[:, cc, 1:1 + SEQ], bank(2 + cc), ACT.Copy).then_inc(L["cu"], 1)

            items, us = ATT[l]
            for i in range(len(us) + 2):
                if i < len(us):
                    u = us[i]
                    act.wait_ge(*L("nm", i + 1))
                    if i >= 4:
                        act.wait_ge(*L("T", us[i - 4].item.m + 1))
                    act.activation(prob[i % 4][:, 0:u.width], bank(2 * (i % 2), u.width), ACT.Exp,
                                   bias=smx[:, 0, i % 8:i % 8 + 1], accum_out=smx[:, 1, i % 8:i % 8 + 1]
                                   ).then_inc(L["exp"], 1)
                if i >= 2 and us[i - 2].item.last == i - 2:
                    it = us[i - 2].item
                    act.wait_ge(*L("T", it.m + 1))
                    if it.m >= 2:
                        act.wait_ge(*L("AV", it.m - 1))
                    n = min(4, len(it.blocks))
                    act.activation(PT[it.m % 2][:, 0:n, :], bank(4, n * P).rearrange("p (a m) -> p a m", a=n),
                                   ACT.Copy).then_inc(L["c4"], 1)
            tq = nq(l) * P
            act.wait_ge(*L("mix", len(items) // 2))
            act.activation(sqd[:, :, 0:tq], hT[:, 6:8, 0:tq], ACT.Square).then_inc(L["dsq"], 1)
            act.wait_ge(*L("dss", 1))
            for cc in range(2):
                ins = act.activation(srt[:, cc, 0:SEQ], bank(2 * cc), ACT.Sqrt, bias=eps[:])
                if l < DEPTH - 1:
                    ins = act.activation(srt[:, cc, SEQ:T], bank(2 * cc + 1, CTX), ACT.Sqrt, bias=eps[:])
            ins.then_inc(L["drt"], 1)

            act.wait_ge(s_acol, 2 * l + 2)
            for i in range(nq(l) + 1):
                if i < nq(l):
                    t = i
                    act.wait_ge(*L("x1", t + 1))
                    if t >= 2:
                        act.wait_ge(*L("ot", t - 1))
                        act.wait_ge(*L(f"stn{t % 2}", 16 * (t // 2)))
                    alink(act, act.activation(o_n[t % 2], o_x[t % 3], ACT.Square, accum_out=stat[:, 0, t:t + 1]))
                    act.activation(stat[:, 1, t:t + 1], stat[:, 0, t:t + 1], ACT.Sqrt, bias=eps[:], scale=1.0 / D
                                   ).then_inc(L["ort"], 1)
                if i >= 1:
                    t, s = i - 1, stream(i - 1)
                    act.wait_ge(*L("ot", t + 1))
                    if t >= 2:
                        act.wait_ge(*L("lg", t - 1))
                    for k in range(4, 8):
                        ins = act.activation(o_h[t % 2][:, k, :], bank(5, P, (k - 4) * P), ACT.Identity,
                                             bias=mod[:, l, 24 + k, s:s + 1], scale=acol[:, l, 1, k, s:s + 1])
                    ins.then_inc(L["oa"], 1)
                if i < nq(l):
                    t = i
                    act.wait_ge(*L("orc", t + 1))
                    act.activation(o_n[t % 2], o_x[t % 3], ACT.Copy, scale=stat[:, 2, t:t + 1]).then_inc(L["oxn"], 1)
            act.wait_ge(*L("asub", 1))
            act.activation(aff[:, 0:nq(l), :], aff[:, 0:nq(l), :], ACT.Exp).then_inc(L["aexp"], 1)
            base = where[("exp", l)]
            with act.Fori(0, NE) as e:
                act.wait_ge(free, e * UNITS_E + (base + 4))
                act.activation(sg, psum[:, 1024:2048].rearrange("p (f m) -> p f m", f=8)[:, :, 0:CAP],
                               ACT.Silu).then_inc(L["silu"], 1)

        for t in range(NX):
            act.wait_ge(f_in[t % 3], 16 * (t // 3 + 1))
            alink(act, act.activation(o_n[t % 2], o_x[t % 3], ACT.Square, accum_out=stat[:, 0, t:t + 1]))
            act.activation(stat[:, 1, t:t + 1], stat[:, 0, t:t + 1], ACT.Sqrt, bias=eps[:], scale=1.0 / D
                           ).then_inc(f_rms, 1)

    @block.tensor
    def _(pe):
        mm, tr = pe.matmul, pe.transpose
        pe.wait_ge(s_const, 1)
        pe.wait_ge(s_cload, 16 * 10)
        tr(bank(0, 62), packr, ident[0:62, 0:62])
        tr(bank(1, 96), packb, ident[0:96, 0:96]).then_inc(s_pack, 1)
        pe.wait_ge(s_cs, 1)

        def ada_mm(gi):
            l, g = ada_order[gi]
            if gi:
                pe.wait_ge(s_col, gi)
            n = where[("ada", l, g)]
            for k in range(KD):
                if k % 4 == 0:
                    arrive(pe, n + k // 4)
                ins = mm(psum[0:2, 7 * 512:], cs[:, k, :], slot(n + k // 4, 4)[:, k % 4, :], start=k == 0,
                         stop=k == KD - 1)
                if k % 4 == 3:
                    ins.then_inc(free, 1)

        def ada_tr(gi):
            pe.wait_ge(s_row, gi + 1)
            for j in range(4):
                ins = tr(bank(7, 2, 2 * j), modrow[:, j * P:(j + 1) * P], ident[0:2, 0:2])
            ins.then_inc(s_adaT, 1)

        for gi in range(4):
            ada_mm(gi)
            ada_tr(gi)

        for l in range(DEPTH):
            L = LS[l]
            last = l == DEPTH - 1
            win = where[("win", l)]
            for i in range(NB + 2):
                if i < NB:
                    t = i
                    pe.wait_ge(*L("xn", t + 1))
                    if t >= 1:
                        pe.wait_ge(*L("hd", t))
                        pe.wait_ge(*L("ha", t))
                    for k in range(KD):
                        ins = tr(bank(k // 4, P, (k % 4) * P), n_n[t % 2][:, k * P:(k + 1) * P], ident[:])
                    ins.then_inc(L["nt"], 1)
                if 1 <= i <= NB:
                    t = i - 1
                    pe.wait_ge(*L("hd", t + 1))
                    pe.wait_ge(*L("ha", t + 1))
                    if t >= 2:
                        pe.wait_ge(*L("kvc", t - 1))
                        pe.wait_ge(*L("rope", min(t - 1, NX)))
                    elif t == 0 and l == 0:
                        pe.wait_ge(s_col, 4)
                    for j in range(3):
                        if last and t >= NX and j < 2:
                            continue
                        if t == 0:
                            arrive(pe, win + j)
                        dst = bank(2 + t % 2, 256, 256 * j) if j < 2 else bank(4 + t % 2, 256)
                        for k in range(KD):
                            ins = mm(dst, hT[:, k, toks(t)], slot(win + j, 8)[:, k, :], start=k == 0, stop=k == KD - 1)
                        if t == (NX if last and j < 2 else NB) - 1:
                            ins.then_inc(free, 1)
                        elif j == 2:
                            ins.then_inc(L["pa"], 1)
                if i >= 2:
                    t = i - 2
                    if t < NX:
                        pe.wait_ge(*L("rope", t + 1))
                    else:
                        pe.wait_ge(*L("kvc", t + 1))
                    if t >= 1:
                        pe.wait_ge(*L("ke", t))
                        pe.wait_ge(*L("qe", min(t, nq(l))))
                    if t < nq(l):
                        for a in range(4):
                            tr(bank(6, P, a * P), rq[t % 2][:, a * P:(a + 1) * P], ident[:])
                    tr(bank(7, P), rk[t % 2], ident[:]).then_inc(L["ta"], 1)
            for i in range(NB + 1):
                if i < NB:
                    t = i
                    if t < 2:
                        pe.wait_ge(*L("kvc", NB - 1 + t))
                    else:
                        pe.wait_ge(*L("vdc", t - 1))
                        pe.wait_ge(*L("ropeb", min(t - 1, NX)))
                    for j in range(3):
                        if last and t >= NX and j < 1:
                            continue
                        if t == 0:
                            arrive(pe, win + 3 + j)
                        dst = bank(2 + t % 2, 256, 256 * j) if j < 2 else bank(4 + t % 2, 256)
                        for k in range(KD):
                            ins = mm(dst, hT[:, k, toks(t)], slot(win + 3 + j, 8)[:, k, :], start=k == 0,
                                     stop=k == KD - 1)
                        if t == (NX if last and j < 1 else NB) - 1:
                            ins.then_inc(free, 1)
                        elif j == 2:
                            ins.then_inc(L["pb"], 1)
                if i >= 1:
                    t = i - 1
                    if t < NX:
                        pe.wait_ge(*L("ropeb", t + 1))
                    else:
                        pe.wait_ge(*L("vdc", t + 1))
                    if t == 0:
                        pe.wait_ge(*L("ke", NB))
                        pe.wait_ge(*L("qe", nq(l)))
                    else:
                        pe.wait_ge(*L("kde", t))
                        pe.wait_ge(*L("qde", min(t, nq(l))))
                    for a in range(0 if t < nq(l) else 2, 4):
                        ins = tr(bank(6 + a // 2, P, (a % 2) * P), rq[t % 2][:, a * P:(a + 1) * P], ident[:])
                    ins.then_inc(L["tb"], 1)
            for j in range(6):
                tile, cc = j // 2, j % 2
                if j < 2:
                    pe.wait_ge(*L("vdc", NB - 1 + j))
                elif j < 4:
                    pe.wait_ge(*L("cu", j - 1))
                else:
                    pe.wait_ge(*L("cuc", j - 3))
                if cc == 0:
                    arrive(pe, win + 6 + tile)
                for part in range(1 if last else 2):
                    t0, t1 = (0, SEQ) if part == 0 else (SEQ, T)
                    for k in range(KD):
                        ins = mm(bank((2 if part == 0 else 4) + cc, t1 - t0), slot(win + 6 + tile, 8)[:, k, cc * P:(cc + 1) * P],
                                 hT[:, k, t0:t1], start=k == 0, stop=k == KD - 1)
                ins.then_inc(free if cc else L["pc"], 1)
            items, us = ATT[l]
            pe.wait_ge(*L("cy", 2))
            pe.wait_ge(*L("kde", NB))
            pe.wait_ge(*L("qde", nq(l)))
            for i in range(len(us) + 3):
                if i < len(us):
                    u, it = us[i], us[i].item
                    if i >= 2:
                        pe.wait_ge(*L("exp", i - 1))
                    b0 = 2 * (i % 2)
                    if it.kind == "D":
                        g = 2 * it.h + u.j
                        q, key = qdT[:, g // 4, toks(it.b)], kdp[:, g, :]
                        if it.b < NX:
                            mm(bank(b0), q, key[:, 0:SEQ], start=True, stop=True)
                            ins = mm(bank(b0 + 1, CTX), q, key[:, SEQ:T], start=True, stop=True)
                        else:
                            ins = mm(bank(b0, CTX), q, key[:, SEQ:T], start=True, stop=True)
                    else:
                        q, key = qT[:, it.h % 4, toks(it.b)], kTp[:, it.h // 4, :]
                        mm(bank(b0, CTX), q, key[:, SEQ:T], start=True, stop=True)
                        near = it.blocks[NC:]
                        if near:
                            t0 = near[0] * P
                            mm(bank(b0, 256, 256), q, key[:, t0:t0 + 256], start=True, stop=False)
                            if len(near) == 3:
                                mm(bank(b0, P, 256), identb[:], masks[:, 0, :], start=False, stop=True)
                                mm(bank(b0 + 1, P), q, key[:, t0 + 256:t0 + 384], start=True, stop=False)
                                mm(bank(b0 + 1, P), identb[:], masks[:, 1, :], start=False, stop=True)
                            elif it.b == 0:
                                mm(bank(b0, P, 384), identb[:], masks[:, 1, :], start=False, stop=True)
                            else:
                                mm(bank(b0, P, 256), identb[:], masks[:, 0, :], start=False, stop=True)
                        ins = mm(bank(b0, 1, u.width - 1), ident[:], sinkb[:, l, it.h:it.h + 1], start=True, stop=True)
                    ins.then_inc(L["S"], 1)
                if 2 <= i < len(us) + 2 and us[i - 2].item.last == i - 2:
                    it = us[i - 2].item
                    pe.wait_ge(*L("diag", it.last + 1))
                    if it.m:
                        pe.wait_ge(*L("c4", it.m))
                        if items[it.m - 1].over:
                            pe.wait_ge(*L("c5", items[it.m - 1].over))
                    for n in range(len(it.blocks)):
                        for uu in range(it.first, it.last + 1):
                            ins = mm(bank(4, P, n * P), prob[uu % 4][:, n * P:(n + 1) * P], diag[:, uu % 4, :],
                                     start=uu == it.first, stop=uu == it.last)
                    ins.then_inc(L["T"], 1)
                if i >= 3 and us[i - 3].item.last == i - 3:
                    it = us[i - 3].item
                    pe.wait_ge(*L("c4", it.m + 1))
                    if it.over:
                        pe.wait_ge(*L("c5", it.over))
                    if it.m % 2 == 0 and it.m:
                        pe.wait_ge(*L("mix", it.m // 2))
                    half = 64 * (it.h % 2)
                    for n, kb in enumerate(it.blocks):
                        v = (vd_sb[:, kb, it.h * 64:it.h * 64 + 64] if it.kind == "D"
                             else v_sb[:, kb, (it.h // 4) * 64:(it.h // 4) * 64 + 64])
                        ins = mm(psum[half:half + 64, 3072:3200], v, PT[it.m % 2][:, n, :], start=n == 0,
                                 stop=n == len(it.blocks) - 1)
                    ins.then_inc(L["AV"], 1)
                if l == 0 and i in ADA_AT:
                    ada_mm(4 + ADA_AT[i])
                if l == 0 and i - 1 in ADA_AT:
                    ada_tr(4 + ADA_AT[i - 1])
            pe.wait_ge(*L("mix", len(items) // 2))
            pe.wait_ge(s_col, len(ada_order))
            for r in range(1 if last else 2):
                for k in range(KD):
                    ins = mm(bank(4 + 2 * r, P, k * P), mod[:, l, 16 + k, r:r + 1].broadcast_to([P, P]), ident[:],
                             start=True, stop=True)
                ins.then_inc(L["gx"], 1)
            pe.wait_ge(*L("dsq", 1))
            for cc in range(2):
                ins = mm(bank(2 * cc), halves[:], sqd[:, cc, 0:SEQ], start=True, stop=True)
                if not last:
                    ins = mm(bank(2 * cc + 1, CTX), halves[:], sqd[:, cc, SEQ:T], start=True, stop=True)
            ins.then_inc(L["dss"], 1)
            pe.wait_ge(*L("gxe", 1))
            for k in range(KD):
                ins = mm(psum[0:CAPX, 2048 + k * P:2048 + (k + 1) * P], mod[:, l, 40 + k, 0:1].broadcast_to([P, CAPX]),
                         ident[:], start=True, stop=True)
                if not last:
                    ins = mm(psum[CAPX:CAP, 2048 + k * P:2048 + (k + 1) * P],
                             mod[:, l, 40 + k, 1:2].broadcast_to([P, CAPC]), ident[:], start=True, stop=True)
            ins.then_inc(L["gx"], 1)
            wo = where[("wout", l)]
            pe.wait_ge(*L("dsub", 1))
            if l == 0:
                pe.wait_ge(s_rout, 16 * DEPTH)
            for i in range(nq(l) + 2):
                if i < nq(l):
                    t = i
                    if t >= 2:
                        pe.wait_ge(*L("x1", t - 1))
                    for k in range(KD):
                        if t == 0 and k % 2 == 0:
                            arrive(pe, wo + k // 2)
                        for n in range(2):
                            ins = mm(bank(2 * (t % 2) + n), mixc(k)[:, toks(t)], slot(wo + k // 2, 2)[:, k % 2, n * 512:(n + 1) * 512],
                                     start=k == 0, stop=k == KD - 1)
                        if t == nq(l) - 1 and k % 2 == 1:
                            ins.then_inc(free, 1)
                    if t < nq(l) - 1:
                        ins.then_inc(L["po"], 1)
                if 1 <= i <= nq(l):
                    t = i - 1
                    pe.wait_ge(*L("oxn", t + 1))
                    if t == 0:
                        pe.wait_ge(*L("gxe", 2 if last else 3))
                    else:
                        pe.wait_ge(*L("od", t))
                        pe.wait_ge(*L("oa", t))
                    for k in range(KD):
                        ins = tr(bank(4, P, k * P), o_n[t % 2][:, k * P:(k + 1) * P], ident[:])
                    ins.then_inc(L["ot"], 1)
                if i >= 2:
                    t = i - 2
                    pe.wait_ge(*L("od", t + 1))
                    pe.wait_ge(*L("oa", t + 1))
                    for k in range(KD):
                        ins = mm(bank(6, NE, t * NE), o_h[t % 2][:, k, :], rout[:, l, k, :], start=k == 0, stop=k == KD - 1)
                    ins.then_inc(L["lg"], 1)
            NR = NE if last else 48
            pe.wait_ge(*L("aff", 1))
            for b in range(NX):
                ins = tr(psum[0:NR, 3584 + b * P:3584 + (b + 1) * P], aff48[:, b, 0:NR], ident[:])
            ins.then_inc(L["aT"], 1)
            pe.wait_ge(*L("pad", 1))
            mm(psum[0:CAP, 3584:3584 + NE], vpad[0:NR, :], sel[0:NR, :], start=True, stop=True)
            mm(psum[0:CAP, 3584 + NE:3584 + 2 * NE], ipad[0:NR, :], sel[0:NR, :], start=True, stop=True
               ).then_inc(L["rows"], 1)
            pe.wait_ge(*L("ri", 1))
            base = where[("exp", l)]

            def arrived(e, q):
                pe.wait_ge(landed[(base + q) % RING], e * 16 + 16 * ((base + q) // RING + 1))

            with pe.Fori(0, NE) as e:
                pe.wait_ge(*L("gat", e * 16 + 16))
                for k in range(KD):
                    ins = tr(bank(0, CAP, k * P), xg[0:CAP, k * P:(k + 1) * P], ident[0:CAP, 0:CAP])
                ins.then_inc(L["xt"], 1)
                pe.wait_ge(*L("xs", e + 1))
                for q in range(8):
                    arrived(e, q)
                    w = slot(base + q, 2)
                    for kk in range(2):
                        k = 2 * (q % 4) + kk
                        for f in range(KF):
                            ins = mm(bank(2 + 2 * (q // 4), CAP, f * P), w[:, kk, f * P:(f + 1) * P], xsT[:, k, :],
                                     start=k == 0 and f % 4 == 0, stop=k == KD - 1, skip_group_check=True)
                    ins.then_inc(free, 1)
                pe.wait_ge(*L("he", e + 1))
                for q in range(8, UNITS_E):
                    arrived(e, q)
                    w = slot(base + q, 2)
                    for kk in range(2):
                        f = 2 * (q - 8) + kk
                        for n in range(2):
                            ins = mm(psum[0:CAP, 3072 + n * 512:3584 + n * 512], hE[:, f, :], w[:, kk, n * 512:(n + 1) * 512],
                                     start=f == 0, stop=f == KF - 1)
                    ins.then_inc(free, 1)

    @block.vector
    def _(dve):
        tt, ts, stt = dve.tensor_tensor, dve.tensor_scalar, dve.scalar_tensor_tensor

        dlink(dve, dve.memset(halves[:], 0.0))
        for h in (0, 64):
            dve.memset(halves[h:h + 64, h:h + 64], 1.0 / HEAD)
        dve.wait_ge(s_pack, 1)
        dve.tensor_copy(bcol[:].rearrange("p l k -> p (l k)"), bank(1, 96))
        dlink(dve, dve.tensor_copy(pack[:], bank(0, 62)))
        for l in range(DEPTH):
            ts(sublc[:, l:l + 1], pack[:, 60 + l:61 + l], 1.0 - lam_init(l), None, ALU.mult)
        lv = lamr.rearrange("p (a two d) -> p a two d", two=2, d=DIFF)
        dlink(dve, tt(lamp[:].rearrange("p l j d -> p (l j) d"), lv[:, :, 0, :], lv[:, :, 1, :], ALU.mult))
        dve.sem_inc(s_packc, 1)
        dve.tensor_reduce(lam2[:].rearrange("p l j -> p (l j)"), lamp[:].rearrange("p l j d -> p (l j) d"),
                          axis=AX_X, op=ALU.add).then_inc(s_lamx, 1)
        dve.wait_ge(s_lam, 1)
        for l in range(DEPTH):
            stt(nlam[:, l:l + 1], lam2[:, l, 1:2], lam_init(l), lam2[:, l, 0:1], ALU.subtract, ALU.subtract)

        def ada_row(gi):
            l, g = ada_order[gi]
            if gi:
                dve.wait_ge(s_adaT, gi)
            dve.wait_ge(free, where[("ada", l, g)] + 2)
            dve.tensor_copy(modrow[:], psum[0:2, 7 * 512:]).then_inc(s_row, 1)

        def ada_col(gi):
            l, g = ada_order[gi]
            dve.wait_ge(s_adaT, gi + 1)
            tt(mod[:, l, 4 * g:4 * g + 4, :], bank(7, 8).rearrange("p (j s) -> p j s", s=2),
               bcol[:, l, 4 * g:4 * g + 4].unsqueeze(2).broadcast_to([P, 4, 2]), ALU.add).then_inc(s_col, 1)
            if g in (3, 9):
                which = 0 if g == 3 else 1
                dve.wait_ge(s_col, gi + 1)
                c0 = 8 if g == 3 else 32
                n0 = 16 + 16 * which + 8 * l
                stt(acol[:, l, which], mod[:, l, c0:c0 + 8, :], 1.0,
                    pack[:, n0:n0 + 8].unsqueeze(2).broadcast_to([P, 8, 2]), ALU.add, ALU.mult).then_inc(s_acol, 1)

        for gi in range(4):
            ada_row(gi)
            ada_col(gi)
        dve.wait_ge(s_acol, 1)

        def swap_sin(src, n, dim, tab, tmp):
            h = dim // 4
            S = tab[:, dim:2 * dim]
            s4 = src.rearrange("p (g ax half i) -> p g ax half i", ax=2, half=2, i=h)
            t4 = tmp.rearrange("p (g ax half i) -> p g ax half i", ax=2, half=2, i=h)
            S4 = S.rearrange("p (ax half i) -> p ax half i", ax=2, half=2)
            for w in range(2):
                tt(t4[:, :, :, w, :], s4[:, :, :, 1 - w, :],
                   S4[:, :, w, :].unsqueeze(1).broadcast_to([P, n, 2, h]), ALU.mult)
            return tab[:, 0:dim]

        for l in range(DEPTH):
            L = LS[l]
            last = l == DEPTH - 1
            dve.wait_ge(*L("tab", 16))
            for i in range(NB + 2):
                if i < NB:
                    t, s = i, stream(i)
                    dve.wait_ge(*L("rt", t + 1))
                    dlink(dve, dve.reciprocal(stat[:, 2, t:t + 1], stat[:, 1, t:t + 1]))
                    if t >= 2:
                        dve.wait_ge(*L("nt", t - 1))
                    ts(n_n[t % 2], n_x[t % 3], stat[:, 2, t:t + 1], None, ALU.mult).then_inc(L["xn"], 1)
                    dve.wait_ge(*L("nt", t + 1))
                    for k in range(4):
                        ins = ts(hT[:, k, toks(t)], bank(0, P, k * P), acol[:, l, 0, k, s:s + 1], mod[:, l, k, s:s + 1],
                                 ALU.mult, ALU.add)
                    ins.then_inc(L["hd"], 1)
                if 1 <= i <= NB and i - 1 < NX:
                    t = i - 1
                    dve.wait_ge(*done_a(l, t))
                    if t >= 2:
                        dve.wait_ge(*L("ta", t - 1))
                    tab = ropet[:, t, 0:2 * HEAD]
                    C = swap_sin(bank(2 + t % 2), HW, HEAD, tab, rtmp)
                    q_out = rq[t % 2].rearrange("p (a s d) -> p s a d", s=2, d=HEAD)
                    dlink(dve, tt(q_out, bank(2 + t % 2).rearrange("p (s a d) -> p s a d", s=2, d=HEAD),
                                  C.unsqueeze(1).unsqueeze(1).broadcast_to([P, 2, 4, HEAD]), ALU.mult))
                    dlink(dve, tt(q_out, q_out, rtmp.rearrange("p (s a d) -> p s a d", s=2, d=HEAD), ALU.add))
                    dve.wait_ge(*L("kvc", t + 1))
                    swap_sin(kraw, NKV, HEAD, tab, rtmp[:, 0:P])
                    k_out = rk[t % 2].rearrange("p (a d) -> p a d", d=HEAD)
                    dlink(dve, tt(k_out, kraw.rearrange("p (a d) -> p a d", d=HEAD),
                                  C.unsqueeze(1).broadcast_to([P, NKV, HEAD]), ALU.mult))
                    tt(rk[t % 2], rk[t % 2], rtmp[:, 0:P], ALU.add).then_inc(L["rope"], 1)
                if i >= 2:
                    t = i - 2
                    dve.wait_ge(*L("kz", 1))
                    dve.wait_ge(*L("ta", t + 1))
                    dve.tensor_copy(kTp[0:64, 0, toks(t)], psum[0:64, 3584:3712])
                    dve.tensor_copy(kTp[64:128, 1, toks(t)], psum[64:128, 3584:3712]).then_inc(L["ke"], 1)
            for i in range(NB + 1):
                if i < NX:
                    t = i
                    dve.wait_ge(*done_b(l, t))
                    if t < 2:
                        dve.wait_ge(*L("ta", NB))
                    else:
                        dve.wait_ge(*L("tb", t - 1))
                    dve.wait_ge(*(L("ropeb", t) if t else L("rope", NX)))
                    C = swap_sin(bank(2 + t % 2), 16, DIFF, ropet[:, t, 2 * HEAD:], rtmp)
                    dlink(dve, tt(rq[t % 2].rearrange("p (g d) -> p g d", d=DIFF),
                                  bank(2 + t % 2).rearrange("p (g d) -> p g d", d=DIFF),
                                  C.unsqueeze(1).broadcast_to([P, 16, DIFF]), ALU.mult))
                    tt(rq[t % 2], rq[t % 2], rtmp, ALU.add).then_inc(L["ropeb"], 1)
                if i >= 1:
                    t = i - 1
                    dve.wait_ge(*L("kz", 2))
                    dve.wait_ge(*L("tb", t + 1))
                    for g in range(4):
                        ins = dve.tensor_copy(kdp[32 * g:32 * g + 32, g::4, toks(t)],
                                              psum[32 * g:32 * g + 32, 3584:3840].rearrange("p (a m) -> p a m", a=2))
                    ins.then_inc(L["kde"], 1)
            for col in (0, PADX - 1, PADX, PADX + PADC - 1):
                ins = dve.memset(upad[:, :, col:col + 1], 0.0)
            W = SEQ if last else PADX + PADC - 2
            for cc in range(2):
                dve.wait_ge(*done_c(l, 2 + cc))
                dve.wait_ge(*L("cu", cc + 1))
                if not last:
                    r = upad[:, cc, PADX + 1:PADX + 1 + CTX]
                    tt(r, r, bank(4 + cc, CTX), ALU.mult)
                r = upad[:, cc, 1:1 + SEQ]
                tt(r, r, bank(2 + cc), ALU.mult).then_inc(L["cuc"], 1)
            dve.wait_ge(*L("cuc", 2))
            for cc in range(2):
                w = [pack[:, 48 + 6 * l + 2 * j + cc:49 + 6 * l + 2 * j + cc] for j in range(CONV_W)]
                dlink(dve, ts(ytmp[:, 0:W], upad[:, cc, 0:W], w[0], None, ALU.mult))
                dlink(dve, stt(ytmp[:, 0:W], upad[:, cc, 1:1 + W], w[1], ytmp[:, 0:W], ALU.mult, ALU.add))
                dlink(dve, stt(ytmp[:, 0:W], upad[:, cc, 2:2 + W], w[2], ytmp[:, 0:W], ALU.mult, ALU.add))
                dve.wait_ge(*done_c(l, 4 + cc))
                if not last:
                    tt(convo[:, cc, SEQ:T], ytmp[:, PADX:PADX + CTX], bank(4 + cc, CTX), ALU.mult)
                tt(convo[:, cc, 0:SEQ], ytmp[:, 0:SEQ], bank(2 + cc), ALU.mult).then_inc(L["cy"], 1)
                dve.wait_ge(*L("cy", cc + 1))
            items, us = ATT[l]
            for i in range(len(us) + 3):
                if i < len(us):
                    dve.wait_ge(*L("S", i + 1))
                    dve.tensor_reduce(smx[:, 0, i % 8:i % 8 + 1], bank(2 * (i % 2), us[i].width), axis=AX_X,
                                      op=ALU.max, negate=True).then_inc(L["nm"], 1)
                if 1 <= i <= len(us):
                    j = i - 1
                    u = us[j]
                    dve.wait_ge(*L("exp", j + 1))
                    dlink(dve, dve.reciprocal(smx[:, 2, j % 8:j % 8 + 1], smx[:, 1, j % 8:j % 8 + 1]))
                    ts(diag[:, j % 4, :], ident[:], smx[:, 2, j % 8:j % 8 + 1], nlam[:, l:l + 1] if u.j else None,
                       ALU.mult, *([ALU.mult] if u.j else [])).then_inc(L["diag"], 1)
                if 2 <= i < len(us) + 2 and us[i - 2].item.last == i - 2 and len(us[i - 2].item.blocks) > 4:
                    it = us[i - 2].item
                    dve.wait_ge(*L("T", it.m + 1))
                    if it.m >= 2:
                        dve.wait_ge(*L("AV", it.m - 1))
                    n = len(it.blocks) - 4
                    dve.tensor_copy(PT[it.m % 2][:, 4:4 + n, :], bank(5, n * P).rearrange("p (a m) -> p a m", a=n)
                                    ).then_inc(L["c5"], 1)
                if i >= 3 and us[i - 3].item.last == i - 3 and us[i - 3].item.m % 2:
                    it = us[i - 3].item
                    dve.wait_ge(*L("AV", it.m + 1))
                    dve.tensor_copy(mixc((6 if it.kind == "D" else 0) + it.h // 2)[:, toks(it.b)], bank(6, P)
                                    ).then_inc(L["mix"], 1)
                if l == 0 and i in ADA_AT:
                    ada_row(4 + ADA_AT[i])
                if l == 0 and i - 1 in ADA_AT:
                    ada_col(4 + ADA_AT[i - 1])
            for r in range(1 if last else 2):
                dve.wait_ge(*L("gx", r + 1))
                dve.tensor_copy(g1row[r], bank(4 + 2 * r, D)).then_inc(L["gxe"], 1)
            tq = nq(l) * P
            dve.wait_ge(*L("drt", 1))
            dlink(dve, dve.reciprocal(srt[:, :, 0:tq], srt[:, :, 0:tq]))
            stt(hT[:, 6:8, 0:tq], hT[:, 6:8, 0:tq], sublc[:, l:l + 1], srt[:, :, 0:tq], ALU.mult, ALU.mult
                ).then_inc(L["dsub"], 1)
            n_tok = CAPX if last else CAP
            dve.wait_ge(*L("gx", 2 if last else 3))
            dve.tensor_copy(g2row[0:n_tok, :], psum[0:n_tok, 2048:3072]).then_inc(L["gxe"], 1)
            for i in range(nq(l) + 1):
                if i < nq(l):
                    t = i
                    dve.wait_ge(*done_o(l, t))
                    dve.wait_ge(*L(f"ox{t % 3}", 16 * (t // 3 + 1)))
                    dlink(dve, tt(o_t, bank(2 * (t % 2), D), g1row[stream(t)], ALU.mult))
                    tt(o_x[t % 3], o_x[t % 3], o_t, ALU.add).then_inc(L["x1"], 1)
                    dve.wait_ge(*L("ort", t + 1))
                    dve.reciprocal(stat[:, 2, t:t + 1], stat[:, 1, t:t + 1]).then_inc(L["orc"], 1)
                if i >= 1:
                    t, s = i - 1, stream(i - 1)
                    dve.wait_ge(*L("ot", t + 1))
                    if t >= 2:
                        dve.wait_ge(*L("lg", t - 1))
                    for k in range(4):
                        ins = ts(o_h[t % 2][:, k, :], bank(4, P, k * P), acol[:, l, 1, k, s:s + 1],
                                 mod[:, l, 24 + k, s:s + 1], ALU.mult, ALU.add)
                    ins.then_inc(L["od"], 1)
            if last:
                dve.memset(xg[CAPX:CAP, :], 0.0)
                dve.memset(xsT[:, :, CAPX:CAP], 0.0)
            nb = nq(l)
            lgt = bank(6, nb * NE).rearrange("p (b e) -> p b e", e=NE)
            av = aff[:, 0:nb, :]

            def per_block(col):
                return affm[:, col, 0:nb].unsqueeze(2).broadcast_to([P, nb, NE])

            dve.wait_ge(*L("lg", nb))
            dlink(dve, dve.tensor_reduce(affm[:, 0, 0:nb], lgt, axis=AX_X, op=ALU.max))
            tt(av, lgt, per_block(0), ALU.subtract).then_inc(L["asub"], 1)
            dve.wait_ge(*L("aexp", 1))
            dlink(dve, dve.tensor_reduce(affm[:, 0, 0:nb], av, axis=AX_X, op=ALU.add))
            dlink(dve, dve.reciprocal(affm[:, 1, 0:nb], affm[:, 0, 0:nb]))
            if not last:
                tt(aff48[:, 0:NC, 32:48], aff[:, NX:NB, :],
                   affm[:, 1, NX:NB].unsqueeze(2).broadcast_to([P, NC, NE]), ALU.mult)
            tt(aff48[:, :, 0:NE], aff[:, 0:NX, :], affm[:, 1, 0:NX].unsqueeze(2).broadcast_to([P, NX, NE]),
               ALU.mult).then_inc(L["aff"], 1)
            NR = NE if last else 48
            wk = work[0:NR, :]
            dve.wait_ge(*L("aT", 1))
            dlink(dve, dve.tensor_copy(wk, psum[0:NR, 3584:4096]))
            for r in range(CAPX // 8):
                v8, i8 = vals[0:NR, 8 * r:8 * r + 8], idx[0:NR, 8 * r:8 * r + 8]
                dlink(dve, dve.max(v8, wk))
                dlink(dve, dve.max_index(i8, v8, wk))
                dlink(dve, dve.match_replace(wk, v8, wk, -1.0))
            dve.tensor_copy(vpad[0:NE, 0:CAPX], vals[0:NE, :])
            if not last:
                dve.tensor_copy(vpad[32:48, CAPX:CAP], vals[32:48, 0:CAPC])
                ts(ipad[32:48, CAPX:CAP], idx[32:48, 0:CAPC], float(SEQ), None, ALU.add)
            dve.tensor_copy(ipad[0:NE, 0:CAPX], idx[0:NE, :]).then_inc(L["pad"], 1)
            dve.wait_ge(*L("rows", 1))
            dve.tensor_copy(gT[:, 0:NE], psum[0:CAP, 3584:3584 + NE])
            dve.tensor_copy(iT[:, NE:NE + 1], psum[0:CAP, 3584 + NE:3585 + NE])
            dve.tensor_copy(iT[:, 0:NE], psum[0:CAP, 3584 + NE:3584 + 2 * NE]).then_inc(L["ri"], 1)
            dve.wait_ge(*L("ri", 1))
            base = where[("exp", l)]
            parts = [(0, 0, CAPX)] if last else [(0, 0, CAPX), (1, CAPX, CAP)]
            xp = psum[:, 0:1024].rearrange("p (k m) -> p k m", k=8)
            up = psum[:, 2048:3072].rearrange("p (f m) -> p f m", f=8)[:, :, 0:CAP]
            with dve.Fori(0, NE) as e:
                dve.wait_ge(*L("xt", e + 1))
                for s, a, b in parts:
                    ins = tt(xsT[:, :, a:b], xp[:, :, a:b], acol[:, l, 1, :, s:s + 1].broadcast_to([P, 8, b - a]), ALU.mult)
                ins.then_inc(L["xm"], 1)
                dve.wait_ge(*L("xm", e + 1))
                for s, a, b in parts:
                    ins = tt(xsT[:, :, a:b], xsT[:, :, a:b], mod[:, l, 24:32, s:s + 1].broadcast_to([P, 8, b - a]), ALU.add)
                ins.then_inc(L["xs"], 1)
                dve.tensor_copy(gcur[:], gT[:, bass.ds(e, 1)]).then_inc(L["gc"], 1)
                dve.wait_ge(free, e * UNITS_E + (base + 8))
                dve.wait_ge(*L("silu", e + 1))
                tt(hE, up, sg, ALU.mult).then_inc(L["he"], 1)
                dve.wait_ge(*L("gc", e + 1))
                dve.wait_ge(*L("yf", e + 1))
                dve.wait_ge(free, e * UNITS_E + (base + 12))
                stt(yg[0:n_tok, :], psum[0:n_tok, 3072:4096], gcur[0:n_tok, :], g2row[0:n_tok, :], ALU.mult, ALU.mult
                    ).then_inc(L["yg"], 1)

        dve.wait_ge(s_nf, 16)
        for t in range(NX):
            dve.wait_ge(f_rms, t + 1)
            dlink(dve, dve.reciprocal(stat[:, 2, t:t + 1], stat[:, 1, t:t + 1]))
            stt(o_x[t % 3], o_x[t % 3], stat[:, 2, t:t + 1], g1row[0], ALU.mult, ALU.mult).then_inc(f_out, 1)

    es.close()

_INS = ["x", "c", "ctx", "c_ctx", "w_ada", "b_ada", "norm1", "norm2", "w_in", "w_out", "attn_sink", "conv_w",
        "diff_lambda", "diff_subln", "router", "w_gate", "w_up", "w_down", "norm_final"]

def kernel(**inputs):
    import concourse.bacc as bacc
    from concourse.bass_utils import run_bass_kernel_spmd

    nc = bacc.Bacc("TRN2", target_bir_lowering=False, num_devices=1)
    arrays = {f"in_{n}": np.ascontiguousarray(inputs[n]) for n in _INS}
    shape = inputs["x"].shape
    arrays["rope_table"] = rope_tables(shape[1])
    args = [nc.dram_tensor(n, a.shape, mybir.dt.from_np(a.dtype), kind="ExternalInput").ap()
            for n, a in arrays.items()]
    args.append(nc.dram_tensor("out_y", shape, F32, kind="ExternalOutput").ap())
    build_program(nc, *args)
    r = run_bass_kernel_spmd(nc, [arrays], core_ids=[0])
    return r.results[0]["out_y"]
```
